# Optimizing a Trainium2 kernel written in Bass

```python
import jax
import jax.numpy as jnp
from jax import lax
import numpy as np

D_MODEL = 1024
BATCH = 1
SEQ = 256
DEPTH = 2
DEC_BATCH = 8
DEC_SEQ = 4
PAST_LEN = 1024
PAGE_SIZE = 128

SGU_GROUPS = 4
SGU_GROUP_DIM = D_MODEL // 8
SGU_DIM = SGU_GROUPS * SGU_GROUP_DIM
CHUNK = 128
MOBA_HEADS = 8
MOBA_HEAD_DIM = D_MODEL // 16
MOBA_DIM = MOBA_HEADS * MOBA_HEAD_DIM
MOBA_BLOCK = 256
MOBA_TOPK = 3
MOBA_Q_CHUNK = 32
MEM_LEN = 256
MEM_HEADS = 4
MEM_HEAD_DIM = D_MODEL // 8
MEM_DIM = MEM_HEADS * MEM_HEAD_DIM
D_FF = ((8 * D_MODEL // 3 + 255) // 256) * 256
ROPE_THETA = 10000.0
NORM_EPS = 1e-6
MASK_VALUE = -1e30
IN_SPLITS = [SGU_DIM, 2 * SGU_DIM, 2 * SGU_DIM + MOBA_DIM, 2 * SGU_DIM + 2 * MOBA_DIM, 2 * SGU_DIM + 3 * MOBA_DIM, 2 * SGU_DIM + 3 * MOBA_DIM + MEM_DIM]
IN_COLS = IN_SPLITS[-1] + 3 * D_MODEL

kernel_name = "hybrid_gmlp_moba_memory_decoder_step"

def rms_norm(x, g):
    xf = x.astype(jnp.float32)
    y = xf * lax.rsqrt(jnp.mean(xf * xf, axis=-1, keepdims=True) + NORM_EPS)
    return (y * g.astype(jnp.float32)).astype(x.dtype)

def layer_norm(x, g, b):
    xf = x.astype(jnp.float32)
    mu = jnp.mean(xf, axis=-1, keepdims=True)
    xc = xf - mu
    y = xc * lax.rsqrt(jnp.mean(xc * xc, axis=-1, keepdims=True) + NORM_EPS)
    return (y * g.astype(jnp.float32) + b.astype(jnp.float32)).astype(x.dtype)

def swiglu(x, w1, w3, w2):
    return (jax.nn.silu(x @ w1) * (x @ w3)) @ w2

def rope(x, pos):
    hd = x.shape[-1]
    half = hd // 2
    inv = ROPE_THETA ** (-jnp.arange(half, dtype=jnp.float32) * 2.0 / hd)
    ang = pos.astype(jnp.float32)[:, None] * inv[None, :]
    cos = jnp.cos(ang)[None, :, None, :].astype(x.dtype)
    sin = jnp.sin(ang)[None, :, None, :].astype(x.dtype)
    x1, x2 = x[..., :half], x[..., half:]
    return jnp.concatenate([x1 * cos - x2 * sin, x2 * cos + x1 * sin], axis=-1)

def chunk_spatial_gate(v, w, b):
    bsz, t_len, _ = v.shape
    n_c = -(-t_len // CHUNK)
    tp = n_c * CHUNK
    vr = jnp.pad(v, ((0, 0), (0, tp - t_len), (0, 0))).reshape(bsz, n_c, CHUNK, SGU_GROUPS, SGU_GROUP_DIM)
    wm = w * jnp.tril(jnp.ones((CHUNK, CHUNK), w.dtype))
    y = jnp.einsum('gij,bcjgd->bcigd', wm, vr) + b.T[None, None, :, :, None]
    return y.reshape(bsz, tp, SGU_DIM)[:, :t_len]

def moba_attention(q, q_pos, k_all, v_all):
    bsz, t_len, n_h, hd = q.shape
    l_len = k_all.shape[1]
    n_blk = -(-l_len // MOBA_BLOCK)
    pad = n_blk * MOBA_BLOCK - l_len
    k_blk = jnp.pad(k_all, ((0, 0), (0, pad), (0, 0), (0, 0))).reshape(bsz, n_blk, MOBA_BLOCK, n_h, hd).transpose(0, 3, 1, 2, 4)
    v_blk = jnp.pad(v_all, ((0, 0), (0, pad), (0, 0), (0, 0))).reshape(bsz, n_blk, MOBA_BLOCK, n_h, hd).transpose(0, 3, 1, 2, 4)
    k_mean = jnp.mean(k_blk.astype(jnp.float32), axis=3)
    n_sel = min(MOBA_TOPK, n_blk)
    scale = hd ** -0.5
    b_i = jnp.arange(bsz)[:, None, None, None]
    h_i = jnp.arange(n_h)[None, :, None, None]
    blk_ids = jnp.arange(n_blk)
    offs = jnp.arange(MOBA_BLOCK)

    def attend(args):
        qc, pc = args
        own = pc // MOBA_BLOCK
        gate = jnp.einsum('bthd,bhnd->bhtn', qc.astype(jnp.float32), k_mean)
        past = blk_ids[None, :] < own[:, None]
        gate = jnp.where(past[None, None], gate, -jnp.inf)
        _, sel = lax.top_k(gate, n_sel)
        own_b = jnp.broadcast_to(own[None, None, :, None], sel.shape[:-1] + (1,)).astype(sel.dtype)
        idx = jnp.concatenate([sel, own_b], axis=-1)
        slot_ok = jnp.concatenate([sel < own_b, jnp.ones(own_b.shape, bool)], axis=-1)
        kg = k_blk[b_i, h_i, idx]
        vg = v_blk[b_i, h_i, idx]
        key_pos = idx[..., None] * MOBA_BLOCK + offs
        ok = slot_ok[..., None] & (key_pos <= pc[None, None, :, None, None])
        s = jnp.einsum('bthd,bhtjsd->bhtjs', qc, kg).astype(jnp.float32) * scale
        s = jnp.where(ok, s, MASK_VALUE)
        p = jax.nn.softmax(s.reshape(s.shape[:3] + (-1,)), axis=-1).reshape(s.shape)
        return jnp.einsum('bhtjs,bhtjsd->bthd', p.astype(vg.dtype), vg)

    qc_len = min(MOBA_Q_CHUNK, t_len)
    n_c = -(-t_len // qc_len)
    tp = n_c * qc_len
    q_p = jnp.pad(q, ((0, 0), (0, tp - t_len), (0, 0), (0, 0)))
    pos_p = jnp.pad(q_pos, (0, tp - t_len), mode='edge')
    q_c = q_p.reshape(bsz, n_c, qc_len, n_h, hd).transpose(1, 0, 2, 3, 4)
    out = lax.map(attend, (q_c, pos_p.reshape(n_c, qc_len)))
    return out.transpose(1, 0, 2, 3, 4).reshape(bsz, tp, n_h, hd)[:, :t_len]

def cross_attention(q, k, v):
    scale = q.shape[-1] ** -0.5
    s = jnp.einsum('bthd,bmhd->bhtm', q, k).astype(jnp.float32) * scale
    p = jax.nn.softmax(s, axis=-1)
    return jnp.einsum('bhtm,bmhd->bthd', p.astype(v.dtype), v)

def memory_kv(mem, g, w):
    m = rms_norm(mem, g) @ w
    mk, mv = jnp.split(m, 2, axis=-1)
    shape = mem.shape[:2] + (MEM_HEADS, MEM_HEAD_DIM)
    return mk.reshape(shape), mv.reshape(shape)

def token_mixing(xn, pos, mem_k, mem_v, past_k, past_v, w_in, ln_g, ln_b, s_w, s_b, w_a, w_b, w_c, w_o):
    bsz, t_len, _ = xn.shape
    h = xn @ w_in
    a_u, a_v, b_q, b_k, b_v, c_q, gates = jnp.split(h, IN_SPLITS, axis=-1)
    u = jax.nn.gelu(a_u, approximate=False)
    v_n = layer_norm(jax.nn.gelu(a_v, approximate=False), ln_g, ln_b)
    y_a = u * chunk_spatial_gate(v_n, s_w, s_b)
    heads = (bsz, t_len, MOBA_HEADS, MOBA_HEAD_DIM)
    q = rope(b_q.reshape(heads), pos)
    k = rope(b_k.reshape(heads), pos)
    v = b_v.reshape(heads)
    if past_k is None:
        k_all, v_all = k, v
    else:
        k_all = jnp.concatenate([past_k, k], axis=1)
        v_all = jnp.concatenate([past_v, v], axis=1)
    y_b = moba_attention(q, pos, k_all, v_all).reshape(bsz, t_len, MOBA_DIM)
    y_c = cross_attention(c_q.reshape(bsz, t_len, MEM_HEADS, MEM_HEAD_DIM), mem_k, mem_v).reshape(bsz, t_len, MEM_DIM)
    g_a, g_b, g_c = jnp.split(jax.nn.sigmoid(gates), 3, axis=-1)
    merged = g_a * (y_a @ w_a) + g_b * (y_b @ w_b) + g_c * (y_c @ w_c)
    return merged @ w_o, k, v, v_n

def setup_inputs(seed: int = 0) -> dict:
    key = jax.random.key(seed)
    ks = iter(jax.random.split(key, 40))
    nrm = lambda shape, scale=1.0: jax.random.normal(next(ks), shape, jnp.float32) * scale
    gain = lambda shape: 1.0 + nrm(shape, 0.02)
    n_pages = PAST_LEN // PAGE_SIZE
    n_used = DEC_BATCH * n_pages
    n_pool = n_used + max(1, n_used // 4)
    kv_page = (DEPTH, n_pool, PAGE_SIZE, MOBA_HEADS, MOBA_HEAD_DIM)
    mem_shape = (DEPTH, DEC_BATCH, MEM_LEN, MEM_HEADS, MEM_HEAD_DIM)
    d_s = D_MODEL ** -0.5
    return {
        'x_prompt': nrm((BATCH, SEQ, D_MODEL)),
        'x_sample': nrm((DEC_BATCH, DEC_SEQ, D_MODEL)),
        'mem_prompt': nrm((BATCH, MEM_LEN, D_MODEL)),
        'cache_k': nrm(kv_page),
        'cache_v': nrm(kv_page),
        'cache_mem_k': nrm(mem_shape),
        'cache_mem_v': nrm(mem_shape),
        'page_table': jax.random.permutation(next(ks), n_pool)[:n_used].reshape(DEC_BATCH, n_pages).astype(jnp.int32),
        'ffn1_norm': gain((DEPTH, D_MODEL)),
        'ffn1_w1': nrm((DEPTH, D_MODEL, D_FF), d_s),
        'ffn1_w3': nrm((DEPTH, D_MODEL, D_FF), d_s),
        'ffn1_w2': nrm((DEPTH, D_FF, D_MODEL), D_FF ** -0.5),
        'mix_norm': gain((DEPTH, D_MODEL)),
        'w_in': nrm((DEPTH, D_MODEL, IN_COLS), d_s),
        'sgu_ln_g': gain((DEPTH, SGU_DIM)),
        'sgu_ln_b': nrm((DEPTH, SGU_DIM), 0.02),
        'sgu_w': nrm((DEPTH, SGU_GROUPS, CHUNK, CHUNK), CHUNK ** -0.5),
        'sgu_b': 1.0 + nrm((DEPTH, SGU_GROUPS, CHUNK), 0.1),
        'mem_norm': gain((DEPTH, D_MODEL)),
        'w_mem_kv': nrm((DEPTH, D_MODEL, 2 * MEM_DIM), d_s),
        'w_a_out': nrm((DEPTH, SGU_DIM, D_MODEL), SGU_DIM ** -0.5),
        'w_b_out': nrm((DEPTH, MOBA_DIM, D_MODEL), MOBA_DIM ** -0.5),
        'w_c_out': nrm((DEPTH, MEM_DIM, D_MODEL), MEM_DIM ** -0.5),
        'w_o': nrm((DEPTH, D_MODEL, D_MODEL), d_s),
        'ffn2_norm': gain((DEPTH, D_MODEL)),
        'ffn2_w1': nrm((DEPTH, D_MODEL, D_FF), d_s),
        'ffn2_w3': nrm((DEPTH, D_MODEL, D_FF), d_s),
        'ffn2_w2': nrm((DEPTH, D_FF, D_MODEL), D_FF ** -0.5),
        'final_norm': gain((D_MODEL,)),
    }

def reference(x_prompt, x_sample, mem_prompt, cache_k, cache_v, cache_mem_k, cache_mem_v, page_table,
              ffn1_norm, ffn1_w1, ffn1_w3, ffn1_w2, mix_norm, w_in, sgu_ln_g, sgu_ln_b, sgu_w, sgu_b,
              mem_norm, w_mem_kv, w_a_out, w_b_out, w_c_out, w_o, ffn2_norm, ffn2_w1, ffn2_w3, ffn2_w2,
              final_norm):
    def layer(x, l, pos, mem_k, mem_v, past_k, past_v):
        x = x + 0.5 * swiglu(rms_norm(x, ffn1_norm[l]), ffn1_w1[l], ffn1_w3[l], ffn1_w2[l])
        mixed, k_new, v_new, sgu_v = token_mixing(
            rms_norm(x, mix_norm[l]), pos, mem_k, mem_v, past_k, past_v, w_in[l], sgu_ln_g[l], sgu_ln_b[l],
            sgu_w[l], sgu_b[l], w_a_out[l], w_b_out[l], w_c_out[l], w_o[l])
        x = x + mixed
        x = x + 0.5 * swiglu(rms_norm(x, ffn2_norm[l]), ffn2_w1[l], ffn2_w3[l], ffn2_w2[l])
        return x, k_new, v_new, sgu_v

    pos_p = jnp.arange(x_prompt.shape[1], dtype=jnp.int32)
    h = x_prompt
    kp, vp, mkp, mvp = [], [], [], []
    for l in range(DEPTH):
        mk, mv = memory_kv(mem_prompt, mem_norm[l], w_mem_kv[l])
        h, k_n, v_n, _ = layer(h, l, pos_p, mk, mv, None, None)
        kp.append(k_n)
        vp.append(v_n)
        mkp.append(mk)
        mvp.append(mv)
    y_prompt = rms_norm(h, final_norm)

    dec_b, n_pages = page_table.shape
    past_len = n_pages * cache_k.shape[2]
    pos_s = past_len + jnp.arange(x_sample.shape[1], dtype=jnp.int32)
    h = x_sample
    ks_, vs_, sv_ = [], [], []
    for l in range(DEPTH):
        past_k = cache_k[l, page_table].reshape(dec_b, past_len, MOBA_HEADS, MOBA_HEAD_DIM)
        past_v = cache_v[l, page_table].reshape(dec_b, past_len, MOBA_HEADS, MOBA_HEAD_DIM)
        h, k_n, v_n, s_v = layer(h, l, pos_s, cache_mem_k[l], cache_mem_v[l], past_k, past_v)
        ks_.append(k_n)
        vs_.append(v_n)
        sv_.append(s_v)
    y_sample = rms_norm(h, final_norm)

    new_k_prompt = jnp.stack(kp)
    new_v_prompt = jnp.stack(vp)
    new_mem_k_prompt = jnp.stack(mkp)
    new_mem_v_prompt = jnp.stack(mvp)
    new_k_sample = jnp.stack(ks_)
    new_v_sample = jnp.stack(vs_)
    new_sgu_v_sample = jnp.stack(sv_)
    return (y_prompt, y_sample, new_k_prompt, new_v_prompt, new_mem_k_prompt, new_mem_v_prompt, new_k_sample, new_v_sample, new_sgu_v_sample)


_drawn_inputs = setup_inputs


def setup_inputs(seed=0):
    import zlib

    import numpy as np

    out = dict(_drawn_inputs(seed))
    spreads = {}
    factors = {'ffn1_norm': 4.58,
     'sgu_ln_g': 8.204,
     'sgu_ln_b': 8.186,
     'mem_norm': 8.037,
     'ffn2_norm': 5.307,
     'final_norm': 7.518,
     'cache_k': 8.0,
     'cache_v': 7.429,
     'cache_mem_k': 5.573,
     'cache_mem_v': 4.358,
     'sgu_b': 6.863}
    for name, (base, spread) in spreads.items():
        noise = np.random.default_rng([zlib.crc32(name.encode()), seed]).standard_normal(out[name].shape)
        drawn = base * np.exp(spread * noise) if base else spread * noise
        out[name] = jnp.asarray(drawn.astype(out[name].dtype))
    for name, factor in factors.items():
        out[name] = (out[name] * factor).astype(out[name].dtype)
    return out
```

```python
from contextlib import ExitStack, contextmanager

import numpy as np
import concourse.bass as bass
from concourse import mybir

F32 = mybir.dt.float32
F32R = mybir.dt.float32r
I32 = mybir.dt.int32
ALU = mybir.AluOpType
ACT = mybir.ActivationFunctionType
AX = mybir.AxisListType
ds = bass.ds

P = 128
D = 1024
KD = D // P
SEQ, DEC_B, DEC_T = 256, 8, 4
NS = DEC_B * DEC_T
T = SEQ + NS
DEPTH = 2
FF = 2816
KF = FF // P
W = 256
SGU = 512
GATE0 = 3072
MEM = 256
PAST = 1024
PAGE = 128
HD = 64
SC_MOBA = HD ** -0.5
SC_MEM = 128 ** -0.5
EPS = 1e-6
NEG = -1e30
UP = FF // W

C_ID, C_ONE, C_SWAP = 0, 128, 256
C_COS, C_SIN = 384, 384 + T
C_CAUSAL = C_SIN + T
C_NEWMASK = C_CAUSAL + 512
C_TRIL = C_NEWMASK + 64
C_REP = C_TRIL + 128
C_BD = C_REP + 32
C_BLOCKW = C_BD + 32
C_EPS = C_BLOCKW + 4
C_ALL = C_EPS + 1

G_FFN1, G_MIX, G_FFN2, G_MEM, G_FINAL, G_LNG, G_LNB, G_ALL = 0, 16, 32, 48, 64, 72, 80, 88


def constants():
    c = np.zeros((P, C_ALL), np.float32)
    p = np.arange(P)
    c[:, C_ID:C_ID + P] = np.eye(P)
    c[:, C_ONE:C_ONE + P] = 1.0
    for m in range(P):
        if m % HD < HD // 2:
            c[m + HD // 2, C_SWAP + m] = -1.0
        else:
            c[m - HD // 2, C_SWAP + m] = 1.0
    pos = np.concatenate([np.arange(SEQ), np.tile(PAST + np.arange(DEC_T), DEC_B)]).astype(np.float32)
    half = HD // 2
    inv = np.float32(10000.0) ** (-np.arange(half, dtype=np.float32) * np.float32(2.0) / np.float32(HD))
    ang = pos[None, :] * inv.astype(np.float32)[p % half][:, None]
    c[:, C_COS:C_COS + T] = np.cos(ang.astype(np.float64))
    c[:, C_SIN:C_SIN + T] = np.sin(ang.astype(np.float64))
    key = np.arange(SEQ)
    for qt in range(2):
        c[:, C_CAUSAL + 256 * qt:C_CAUSAL + 256 * qt + 256] = np.where(key[None, :] <= p[:, None] + P * qt, 0.0, NEG)
    k = np.arange(NS)
    for g in range(2):
        ok = (k[None, :] // DEC_T == 4 * g + p[:, None] // 32) & (k[None, :] % DEC_T <= p[:, None] % DEC_T)
        c[:, C_NEWMASK + 32 * g:C_NEWMASK + 32 * g + 32] = np.where(ok, 0.0, NEG)
    c[:, C_TRIL:C_TRIL + P] = p[:, None] <= p[None, :]
    for j in range(DEC_T):
        c[j, C_REP + np.arange(NS)[np.arange(NS) % DEC_T == j]] = 1.0
    c[:NS, C_BD:C_BD + NS] = (k[:, None] // DEC_T == k[None, :] // DEC_T)
    c[:, C_BLOCKW:C_BLOCKW + 4] = np.arange(1, 5)
    c[:, C_EPS] = EPS
    return c


class Count:

    def __init__(self, n=0):
        self.n, self.terms = n, []

    def at(self, ahead=0):
        v = self.n + ahead
        for reg, stride in self.terms:
            v = reg * stride + v
        return v

    def next(self):
        self.n += 1
        return self.at()


@contextmanager
def repeat(eng, trips, strides):
    start = {c: c.n for c in strides}
    with eng.Fori(0, trips) as i:
        for c, s in strides.items():
            c.terms.append((i, s))
        yield i
    for k, (c, s) in enumerate(strides.items()):
        c.terms.pop()
        assert c.n - start[c] == s, f"count {k} moves by {c.n - start[c]} in a turn, not {s}"
        c.n = start[c] + trips * s


PAIRS = 56
RES = 48
SUMS = 5
OCTETS = 20
STEPS = 54
HEADS = 12
SOFT = HEADS + 4


def bank_schedule():
    pro = [("gainT", 2)] + [(f"in{t}_{q}", q) for t in range(5) for q in range(2)]
    layer = [("mk0", 0), ("mk1", 1), ("mv0", 0), ("mv1", 1), ("wmT", 2), ("rep", 2)]
    layer += [(f"rotq{c}", c % 3) for c in range(4)] + [(f"rotk{c}", (c + 1) % 3) for c in range(4)]
    layer += [(f"vn{t}", t) for t in range(3)] + [(f"sgu{g}", g % 3) for g in range(4)]
    layer += [(f"k{t}", t) for t in range(3)] + [(f"v{t}", t) for t in range(3)]
    for n in range(HEADS + 2):
        if n < HEADS:
            layer.append((f"S{n}", 0))
        if 1 <= n <= HEADS:
            layer.append((f"PT{n - 1}", 1))
        if n >= 2 and (n - 2 >= 8 or (n - 2) % 2 == 0):
            layer.append((f"O{n - 2}", 2))
    octet = [(f"kT{e}", e % 2) for e in range(8)] + [("sS", 2)]
    layer.append(("loop", 2, [("loop", 4, octet), ("newS", 2), ("pT0", 0), ("pT1", 1), ("pTn", 0), ("oG", 2), ("oT", 1)]))
    layer += [(f"mkT0_{e}", e % 2) for e in range(8)] + [("ms0", 2)] + [(f"mkT1_{e}", e % 2) for e in range(8)] + [("ms1", 2)]
    layer += [("mpT0", 0), ("mpT1", 1), ("mo0", 2), ("mo1", 0), ("moT0", 1), ("moT1", 2)]
    fin = [(f"out{t}_{q}", q) for t in range(3) for q in range(2)]
    return pro + [("loop", DEPTH, layer)] + fin


BY_PAGES = ("sS", "oG", "ms0", "ms1", "mo0", "mo1")


def number_banks(items, start, strides, table, left_out=()):
    n = list(start)
    for it in items:
        if it[0] == "loop":
            body = number_banks(it[2], [0, 0, 0], [], {}, left_out)
            number_banks(it[2], n, strides + [body], table, left_out)
            n = [n[b] + it[1] * body[b] for b in range(3)]
        elif it[0] not in left_out:
            n[it[1]] += 1
            table[it[0]] = (it[1], n[it[1]], [s[it[1]] for s in strides])
    return n


def build(nc, A):
    st = ExitStack()
    base = [16512]

    def at(name, shape, dt, offset):
        return nc.alloc_sbuf_tensor_at(name, shape, dt, offset=offset)

    def sb(name, shape, dt=F32):
        o = base[0]
        base[0] += (int(np.prod(shape[1:])) * 4 + 31) // 32 * 32
        assert base[0] <= 229344, (name, base[0])
        return at(name, shape, dt, o)

    def sem(name):
        return st.enter_context(nc.semaphore(name))

    wraw = [sb(f"wraw{u}", [P, 4, W]) for u in range(4)]
    whi = [sb(f"whi{u}", [P, 4, W], F32R) for u in range(4)]
    wlo = [sb(f"wlo{u}", [P, 4, W], F32R) for u in range(4)]
    x = sb("x_T", [P, KD, T])
    work_at = base[0]
    work = sb("work", [P, KD, T])
    nh = sb("norm_hi", [P, KD, T], F32R)
    nl = sb("norm_lo", [P, KD, T], F32R)
    hh_at = base[0]
    hh = sb("h_hi", [P, KF, T], F32R)
    hl_at = base[0]
    hl = sb("h_lo", [P, KF, T], F32R)
    cst = sb("consts", [P, C_ALL])
    gains = sb("gains", [P, G_ALL])
    memn = sb("memn_T", [P, KD, MEM])
    u_at = base[0]
    u_t = sb("u_T", [P, 4, T])
    gv = sb("gv_T", [P, 4, T])
    qk = sb("qk_T", [P, 8, T])
    cq = sb("cq_T", [P, 4, T])
    rows_at = base[0]
    rows_a = sb("rows_a", [P, 3, 512])
    vrows_at = base[0]
    vrows = sb("v_rows", [P, 3, 512])
    mkT = sb("mk_T", [P, 4, MEM])
    mvrow = sb("mv_rows", [P, 2, 512])
    wmT = sb("sgu_wT", [P, 4, P])
    sgb = sb("sgu_bias", [P, 4, P])
    sil_at = base[0]
    sil = sb("sil", [P, 2, T])
    hf_at = base[0]
    hf = sb("hf", [P, 2, T])
    std_at = base[0]
    std = sb("std", [P, T])
    rstd = sb("rstd", [P, T])
    bd = sb("sgu_blockdiag", [NS, 4, NS])
    stat = sb("stat", [P, 48])
    ptab = sb("page_ids", [1, DEC_B * 8], I32)
    soft0 = sb("soft0", [P, 2, 256])
    ptp0 = sb("probs_T0", [P, 4, P])
    tail_hi = hh_at + 12 * T * 4
    tail_lo = hl_at + 12 * T * 4
    soft = [soft0, at("soft1", [P, 2, 256], F32, hf_at)]
    ptp = [ptp0, at("probs_T1", [P, 4, P], F32, sil_at)]
    page = [at(f"page{e}", [P, 512], F32, tail_hi + 2048 * e if e < 4 else work_at + 2048 * (e - 4)) for e in range(8)]
    kTb = [at("kT0", [P, 4, P], F32, tail_hi + 8192), at("kT1", [P, 4, P], F32, tail_lo)]
    qbd = [at(f"q_blockdiag{g}", [P, 4, 4, 32], F32, sil_at + 2048 * g) for g in range(2)]
    S = at("scores", [P, 1056], F32, tail_lo + 2048)
    PT = at("past_probs_T", [P, 9, P], F32, tail_lo + 2048 + 4224)
    acc = at("merged", [P, KD, T], F32, u_at)
    gsil = at("gate_sigmoid", [P, 2, T], F32, rows_at)
    gtmp = at("gated", [P, 2, T], F32, std_at)
    krows = at("k_rows", [P, 3, 512], F32, tail_hi)
    rtmp = [at("rot0", [P, T], F32, sil_at), at("rot1", [P, T], F32, sil_at + 1152)]
    lnsq = at("ln_square", [P, 4, T], F32, vrows_at)
    swrow = at("sgu_w_rows", [P, 4, P], F32, hf_at)
    xrow = [at("xrow0", [P, 1024], F32, tail_hi), at("xrow1", [P, 1024], F32, tail_hi + 4096),
            at("xrow2", [P, 1024], F32, work_at), at("mrow0", [P, 1024], F32, work_at + 4096),
            at("mrow1", [P, 1024], F32, tail_lo)]
    grow = at("gain_rows", [G_ALL, P], F32, tail_lo + 4096)
    yout = [at("yout0", [P, 1024], F32, tail_hi), at("yout1", [P, 1024], F32, tail_hi + 4096),
            at("yout2", [P, 1024], F32, tail_lo)]

    ident = cst[:, C_ID:C_ID + P]
    ones = cst[:, C_ONE:C_ONE + P]
    swap = cst[:, C_SWAP:C_SWAP + P]
    epsc = cst[:, C_EPS:C_EPS + 1]

    res = st.enter_context(nc.psum_tensor("res", [P, 4, 512], F32))
    bank = [st.enter_context(nc.psum_tensor(f"bank{b}", [P, 512], F32)) for b in range(3)]
    sums = st.enter_context(nc.psum_tensor("sums", [P, 512], F32))

    def rs(s, n=T):
        return res[:, 2 * s:2 * s + 2, 0:n]

    raw_loaded = [sem(f"raw_loaded{u}") for u in range(4)]
    hi_done = [sem(f"hi_done{u}") for u in range(4)]
    lo_done = [sem(f"lo_done{u}") for u in range(4)]
    w_used = [sem(f"w_used{u}") for u in range(4)]
    evac = [sem(f"evac{s}") for s in range(2)]
    h_hi = sem("h_hi_done")
    h_ready = sem("h_ready")
    sq_ready = sem("sq_ready")
    sum_done = sem("sum_done")
    sum_read = sem("sum_read")
    nf_ready = sem("nf_ready")
    nh_ready = sem("nh_ready")
    norm_ready = sem("norm_ready")
    memn_ready = sem("memn_ready")
    mem_hi = sem("mem_hi")
    mem_ready = sem("mem_ready")
    xc_sq = sem("xc_squares")
    vn_ready = sem("vn_ready")
    filled = [sem(f"bank_filled{b}") for b in range(3)]
    emptied = [sem(f"bank_emptied{b}") for b in range(3)]
    rot_ready = sem("rot_ready")
    ya_ready = sem("ya_ready")
    y_hi = sem("y_hi")
    y_lo = sem("y_lo")
    m_f = sem("merged")
    m_hi = sem("merged_hi")
    m_lo = sem("merged_lo")
    qbd_ready = sem("qbd_ready")
    p_max = sem("row_max")
    p_exp = sem("probs_exp")
    p_nrm = sem("probs_normal")
    page_loaded = [sem(f"page_loaded{e}") for e in range(8)]
    page_used = [sem(f"page_used{e}") for e in range(8)]
    dve_step = sem("dve_step")
    ld_const = sem("ld_const")
    ld_gain = sem("ld_gain")
    ld_x = [sem(f"ld_x{i}") for i in range(5)]
    ld_page = sem("ld_page_ids")
    ld_sw = sem("ld_sgu_w")
    ld_sb = sem("ld_sgu_b")
    out_mem, out_vn, out_k, out_v, out_y = (sem(n) for n in ("out_mem", "out_vn", "out_k", "out_v", "out_y"))

    banks, fills = {}, {}
    number_banks(bank_schedule(), [1, 1, 1], [], banks)
    number_banks(bank_schedule(), [0, 0, 0], [], fills, BY_PAGES)

    def bk(name):
        return bank[banks[name][0]]

    def ordinal(name, regs, table):
        _, n, strides = table[name]
        assert len(regs) == len(strides), name
        for r, s in zip(regs, strides):
            n = r * s + n
        return n

    def fill(name, *regs):
        return filled[banks[name][0]], ordinal(name, regs, fills)

    def empty(name, *regs):
        return emptied[banks[name][0]], ordinal(name, regs, banks)

    def filled_of(name):
        return filled[banks[name][0]]

    def emptied_of(name):
        return emptied[banks[name][0]]

    wt = {n: A[n].rearrange("l (k p) f -> l p k f", p=P) for n in (
        "ffn1_w1", "ffn1_w3", "ffn1_w2", "ffn2_w1", "ffn2_w3", "ffn2_w2", "w_in", "w_mem_kv", "w_a_out", "w_b_out",
        "w_c_out", "w_o")}
    branch_w = ["w_a_out", "w_b_out", "w_c_out"]
    DOWN_NK = [8, 8, 6]
    DOWN_PAIRS = [(DOWN_NK[2 * p % 3], DOWN_NK[(2 * p + 1) % 3]) for p in range(6)]
    FULL, MERGE = (8, 8), (8, 4)

    block = st.enter_context(nc.Block())

    @block.tensor
    def _(pe):
        used = Count(1)
        r = [Count(1), Count(1)]
        nsum = Count()
        nsq = Count()
        nrm = Count()
        hcnt = Count(1)
        soft_n = Count()
        octet = Count()

        def wait(sem_value):
            pe.wait_ge(*sem_value)

        def free(name, *regs):
            s, n = empty(name, *regs)
            pe.wait_ge(s, n - 1)

        def tile(s, nk, moving, n=T, ready=None, halves=(0, 1)):
            if 0 in halves:
                pe.wait_ge(evac[s], r[s].at())
            for h in halves:
                u, kh = 2 * s + h, nk // 2
                pe.wait_ge(lo_done[u], used.at(1))
                if ready:
                    ready(h)
                for c in range(2):
                    for k in range(kh):
                        hi, lo = moving(h * kh + k)
                        a, b = whi[u][:, k, c * P:(c + 1) * P], wlo[u][:, k, c * P:(c + 1) * P]
                        for i, (w_, m_) in enumerate(((a, hi), (a, lo), (b, hi))):
                            mm = pe.matmul(res[:, 2 * s + c, 0:n], w_, m_, start=h == 0 and k == 0 and i == 0,
                                           stop=h == 1 and k == kh - 1 and i == 2)
                mm.then_inc(w_used[u], 1)
            if 1 in halves:
                r[s].next()
                if s == 1:
                    used.next()

        def normed(k):
            return nh[:, k, :], nl[:, k, :]

        def norm_wait(h):
            pe.wait_ge(norm_ready, nrm.at(2 * h + 2))

        def sum_squares(g, last_g=3, n=T):
            if g == 0:
                pe.wait_ge(sum_read, nsum.at()) if not isinstance(nsum.at(), int) or nsum.at() > 0 else None
            pe.wait_ge(sq_ready, nsq.next())
            for k in (2 * g, 2 * g + 1):
                mm = pe.matmul(sums[:, 0:n], ones, work[:, k, 0:n], start=k == 0, stop=k == 2 * last_g + 1)
            if g == last_g:
                mm.then_inc(sum_done, 1)
                nsum.next()

        def ffn():
            with repeat(pe, UP, {used: 1, r[0]: 1, r[1]: 1}):
                tile(0, 8, normed, ready=norm_wait)
                tile(1, 8, normed)
            nrm.n += 4
            for t in range(12):
                g, part = t // 3, t % 3
                nk = DOWN_NK[part]
                tile_down(t, g, part, nk)
                if part == 2 and g:
                    sum_squares(g - 1)
            sum_squares(3)
            hcnt.n += UP

        def tile_down(t, g, part, nk):
            s = t % 2
            ps = g % 2
            if part == 0:
                pe.wait_ge(evac[ps], r[ps].at())
            for h in range(2):
                u, kh = 2 * s + h, nk // 2
                pe.wait_ge(lo_done[u], used.at(1))
                kmax = 8 * part + h * kh + kh - 1
                if g == 0:
                    pe.wait_ge(h_ready, hcnt.at(kmax // 2 + 1))
                for c in range(2):
                    for k in range(kh):
                        kk = 8 * part + h * kh + k
                        a, b = whi[u][:, k, c * P:(c + 1) * P], wlo[u][:, k, c * P:(c + 1) * P]
                        for i, (w_, m_) in enumerate(((a, hh[:, kk, :]), (a, hl[:, kk, :]), (b, hh[:, kk, :]))):
                            mm = pe.matmul(res[:, 2 * ps + c, 0:T], w_, m_,
                                           start=part == 0 and h == 0 and k == 0 and i == 0,
                                           stop=part == 2 and h == 1 and k == kh - 1 and i == 2)
                mm.then_inc(w_used[u], 1)
            if part == 2:
                r[ps].next()
            if s == 1:
                used.next()

        def transposes(name, regs, src, dst_cols):
            free(name, *regs)
            for (d, i_) in zip(dst_cols, src):
                mm = pe.transpose(d, i_, ident[0:i_.shape[0], 0:i_.shape[0]])
            mm.then_inc(filled_of(name), 1)

        def rows(name, L, src, t):
            c0, m = t * P, (P if t < 2 else NS)
            b = bk(name)
            transposes(name, (L,), [src[:, c, c0:c0 + m] for c in range(4)], [b[0:m, c * P:(c + 1) * P] for c in range(4)])

        def rotate(L, which, c):
            name = f"rot{which}{c}"
            free(name, L)
            o = 0 if which == "q" else 4
            pe.matmul(bk(name)[:, 0:T], swap, work[:, o + c, :], start=True, stop=True).then_inc(filled_of(name), 1)

        pe.wait_ge(ld_const, 16)
        pe.wait_ge(ld_gain, 7 * 16)
        pe.transpose(bk("gainT")[:, 0:G_ALL], grow[:], ident[0:G_ALL, 0:G_ALL]).then_inc(filled_of("gainT"), 1)
        for t in range(5):
            pe.wait_ge(ld_x[t], 16)
            m = NS if t == 2 else P
            for q in range(2):
                b = bk(f"in{t}_{q}")
                transposes(f"in{t}_{q}", (), [xrow[t][0:m, (4 * q + c) * P:(4 * q + c + 1) * P] for c in range(4)],
                           [b[:, c * P:c * P + m] for c in range(4)])
        pe.wait_ge(sq_ready, nsq.next())
        for k in range(8):
            mm = pe.matmul(sums[:, 0:MEM], ones, work[:, k, 0:MEM], start=k == 0, stop=k == 7)
        mm.then_inc(sum_done, 1)
        nsum.next()
        for g in range(4):
            sum_squares(g)

        with repeat(pe, DEPTH, {used: PAIRS, r[0]: RES, r[1]: RES, nsum: SUMS, nsq: 12, nrm: 12, hcnt: 2 * UP,
                                soft_n: SOFT, octet: OCTETS}) as L:
            ffn()

            def memory(k):
                return hh[:, k, 0:MEM], hl[:, k, 0:MEM]
            for t in range(4):
                tile(t % 2, 8, memory, n=MEM,
                     ready=(lambda h: pe.wait_ge(mem_ready, L * 4 + (2 * h + 2))) if t == 0 else None)

            def w_in_pair(j):
                tile(0, 8, normed, ready=norm_wait if j == 0 else None)
                tile(1, 8, normed)
            w_in_pair(0)
            nrm.n += 4
            pe.wait_ge(evac[0], r[0].at(-1))
            pe.wait_ge(evac[1], r[1].at(-1))
            for nm, src in (("mk", mkT), ("mv", work)):
                for t in range(2):
                    rows(f"{nm}{t}", L, src, t)
            pe.wait_ge(ld_sw, L * 16 + 16)
            transposes("wmT", (L,), [swrow[:, g, :] for g in range(4)],
                       [bk("wmT")[:, g * P:(g + 1) * P] for g in range(4)])
            w_in_pair(1)
            wait(empty("wmT", L))
            free("rep", L)
            pe.matmul(bk("rep")[0:NS, 0:16].rearrange("p (g i) -> p g i", g=4), cst[:, C_REP:C_REP + NS],
                      wmT[:, :, 0:4], start=True, stop=True).then_inc(filled_of("rep"), 1)
            w_in_pair(2)
            pe.wait_ge(sum_read, nsum.at())
            pe.wait_ge(evac[1], r[1].at(-1))
            for k in range(4):
                mm = pe.matmul(sums[:, 0:T], ones, gv[:, k, :], start=k == 0, stop=k == 3)
            mm.then_inc(sum_done, 1)
            nsum.next()
            w_in_pair(3)
            pe.wait_ge(xc_sq, L + 1)
            pe.wait_ge(sum_read, nsum.at())
            for k in range(4):
                mm = pe.matmul(sums[:, 0:T], ones, lnsq[:, k, :], start=k == 0, stop=k == 3)
            mm.then_inc(sum_done, 1)
            nsum.next()
            pe.wait_ge(evac[0], r[0].at())
            pe.wait_ge(evac[1], r[1].at())
            for c in range(4):
                rotate(L, "q", c)
            w_in_pair(4)
            for c in range(4):
                rotate(L, "k", c)
            w_in_pair(5)
            pe.wait_ge(vn_ready, L + 1)
            for t in range(3):
                rows(f"vn{t}", L, gv, t)
            wait(empty("rep", L))
            for t in range(3):
                wait(empty(f"vn{t}", L))
            for g in range(4):
                nm = f"sgu{g}"
                free(nm, L)
                for t in range(2):
                    pe.matmul(bk(nm)[:, t * P:(t + 1) * P], rows_a[:, t, g * P:(g + 1) * P], wmT[:, g, :],
                              start=True, stop=True)
                pe.matmul(bk(nm)[:, SEQ:T], rows_a[0:NS, 2, g * P:(g + 1) * P], bd[:, g, :],
                          start=True, stop=True).then_inc(filled_of(nm), 1)
            pe.wait_ge(rot_ready, L * 8 + 8)
            for t in range(3):
                rows(f"k{t}", L, qk[:, 4:8, :], t)
            pe.wait_ge(evac[1], r[1].at(-1))
            for t in range(3):
                rows(f"v{t}", L, work, t)

            def head_scores(n):
                nm = f"S{n}"
                free(nm, L)
                for qt in range(2):
                    if n < 8:
                        c, lo = n // 2, HD * (n % 2)
                        lhs = qk[lo:lo + HD, c, qt * P:(qt + 1) * P]
                        rhs = qk[lo:lo + HD, 4 + c, 0:SEQ]
                    else:
                        c = n - 8
                        lhs, rhs = cq[:, c, qt * P:(qt + 1) * P], mkT[:, c, :]
                    mm = pe.matmul(bk(nm)[:, qt * 256:(qt + 1) * 256], lhs, rhs, start=True, stop=True)
                mm.then_inc(filled_of(nm), 1)

            def head_turn(n):
                nm = f"PT{n}"
                pe.wait_ge(p_nrm, soft_n.at(n + 1))
                blocks = [(0, 0), (1, 0), (1, 1)] if n < 8 else [(0, 0), (1, 0), (0, 1), (1, 1)]
                transposes(nm, (L,), [soft[n % 2][:, qt, kt * P:(kt + 1) * P] for qt, kt in blocks],
                           [bk(nm)[:, i * P:(i + 1) * P] for i in range(len(blocks))])

            def head_out(n):
                pt = ptp[n % 2]
                wait(empty(f"PT{n}", L))
                if n < 8:
                    nm, lo = f"O{n - n % 2}", HD * (n % 2)
                    if n % 2 == 0:
                        free(nm, L)
                    o = bk(nm)[lo:lo + HD, 0:SEQ]
                    v0, v1 = (vrows[:, t, n * HD:(n + 1) * HD] for t in range(2))
                    pe.matmul(o, v0, pt[:, 0:2, :], start=True, stop=False)
                    mm = pe.matmul(bk(nm)[lo:lo + HD, P:SEQ], v1, pt[:, 2, :], start=False, stop=True)
                    if n % 2:
                        mm.then_inc(filled_of(nm), 1)
                else:
                    nm, c = f"O{n}", n - 8
                    free(nm, L)
                    for t in range(2):
                        mm = pe.matmul(bk(nm)[:, 0:SEQ], mvrow[:, t, c * P:(c + 1) * P], pt[:, 2 * t:2 * t + 2, :],
                                       start=t == 0, stop=t == 1)
                    mm.then_inc(filled_of(nm), 1)

            for t in range(3):
                wait(empty(f"v{t}", L))
            def branch(j):
                return lambda k: (hh[:, 4 * j + k, :], hl[:, 4 * j + k, :])

            def gate_step(m):
                if m % 3 < 2:
                    tile(0, 8, normed, halves=(m % 3,))
                else:
                    tile(1, 4, branch(0), ready=lambda h: pe.wait_ge(y_lo, L * 3 + 1))

            for n in range(HEADS + 2):
                if n < HEADS:
                    head_scores(n)
                    gate_step(n)
                if 1 <= n <= HEADS:
                    head_turn(n - 1)
                if n >= 2:
                    head_out(n - 2)
            soft_n.n += HEADS

            def page_turn(e, name, *regs):
                pe.wait_ge(page_loaded[e], octet.at(1) * 16)
                transposes(name, regs, [page[e][:, c * P:(c + 1) * P] for c in range(4)],
                           [bk(name)[:, c * P:(c + 1) * P] for c in range(4)])

            def page_scores(e, turned, regs, q_, out):
                wait(empty(turned, *regs))
                for c in range(4):
                    mm = pe.matmul(out, q_[:, c], kTb[e % 2][:, c, :], start=c == 0, stop=c == 3)
                mm.then_inc(page_used[e], 1)

            def own_heads(name, regs, rows_):
                free(name, *regs)
                for c in range(4):
                    mm = pe.matmul(bk(name)[:, c * 32:(c + 1) * 32].rearrange("p (b r) -> p b r", b=4),
                                   rows_[:, c * P:(c + 1) * P],
                                   ident.rearrange("p (b r) -> p b r", b=4)[:, :, 8 * c:8 * c + 8], start=True, stop=True)
                mm.then_inc(filled_of(name), 1)

            with repeat(pe, 2, {soft_n: 1, octet: 8}) as G:
                with repeat(pe, 4, {octet: 1}) as jj:
                    for e in range(9):
                        if e < 8:
                            page_turn(e, f"kT{e}", L, G, jj)
                        if e == 1:
                            free("sS", L, G, jj)
                            pe.wait_ge(qbd_ready, L * 4 + (G + 1))
                        if e:
                            par, bb = (e - 1) // 4, (e - 1) % 4
                            page_scores(e - 1, f"kT{e - 1}", (L, G, jj), qbd[0][:, :, bb, :],
                                        bk("sS")[32 * bb:32 * bb + 32, par * P:(par + 1) * P])
                    octet.next()
                free("newS", L, G)
                for bb in range(4):
                    for c in range(4):
                        mm = pe.matmul(bk("newS")[32 * bb:32 * bb + 32, 0:NS], qbd[0][:, c, bb, :], qk[:, 4 + c, SEQ:T],
                                       start=c == 0, stop=c == 3)
                mm.then_inc(filled_of("newS"), 1)
                pe.wait_ge(p_nrm, soft_n.next())
                for i in range(2):
                    transposes(f"pT{i}", (L, G), [S[:, (4 * i + j) * P:(4 * i + j + 1) * P] for j in range(4)],
                               [bk(f"pT{i}")[:, j * P:(j + 1) * P] for j in range(4)])
                transposes("pTn", (L, G), [S[:, PAST:PAST + NS]], [bk("pTn")[0:NS, 0:P]])
                free("oG", L, G)
                for nm in ("pT1", "pTn"):
                    wait(empty(nm, L, G))

                def out_rows(bb):
                    return bk("oG")[32 * bb:32 * bb + 32, :]
                for jj in range(4):
                    for e in range(8):
                        par, bb = e // 4, e % 4
                        pe.wait_ge(page_loaded[e], octet.at(1) * 16)
                        pe.matmul(out_rows(bb), PT[:, jj * 2 + par, 32 * bb:32 * bb + 32], page[e][:],
                                  start=jj == 0 and par == 0, stop=jj == 3 and par == 1).then_inc(page_used[e], 1)
                        if jj == 0 and par == 0:
                            pe.matmul(out_rows(bb), PT[0:NS, 8, 32 * bb:32 * bb + 32], vrows[0:NS, 2, :],
                                      start=False, stop=False)
                    octet.next()
                wait(empty("oG", L, G))
                own_heads("oT", (L, G), S[:, 0:512])

            for g in range(2):
                for e in range(9):
                    if e < 8:
                        page_turn(e, f"mkT{g}_{e}", L)
                    if e == 1:
                        free(f"ms{g}", L)
                        pe.wait_ge(qbd_ready, L * 4 + (3 + g))
                    if e:
                        bb, mt = (e - 1) // 2, (e - 1) % 2
                        page_scores(e - 1, f"mkT{g}_{e - 1}", (L,), qbd[g][:, :, bb, :],
                                    bk(f"ms{g}")[32 * bb:32 * bb + 32, mt * P:(mt + 1) * P])
                octet.next()
            for g in range(2):
                pe.wait_ge(p_nrm, soft_n.next())
                transposes(f"mpT{g}", (L,), [S[:, g * MEM + i * P:g * MEM + (i + 1) * P] for i in range(2)],
                           [bk(f"mpT{g}")[:, i * P:(i + 1) * P] for i in range(2)])
            for g in range(2):
                wait(empty(f"mpT{g}", L))
                free(f"mo{g}", L)
                for e in range(8):
                    bb, mt = e // 2, e % 2
                    pe.wait_ge(page_loaded[e], octet.at(1) * 16)
                    pe.matmul(bk(f"mo{g}")[32 * bb:32 * bb + 32, :], PT[:, 2 * g + mt, 32 * bb:32 * bb + 32], page[e][:],
                              start=mt == 0, stop=mt == 1).then_inc(page_used[e], 1)
                octet.next()
            for g in range(2):
                wait(empty(f"mo{g}", L))
                own_heads(f"moT{g}", (L,), S[:, 512 * g:512 * g + 512])

            for j in (1, 2):
                with repeat(pe, 4, {used: 1, r[0]: 1, r[1]: 1}):
                    tile(0, 8, normed)
                    tile(1, 4, branch(j), ready=lambda h: pe.wait_ge(y_lo, L * 3 + (j + 1)))
            def merged(k):
                return hh[:, 12 + k, :], hl[:, 12 + k, :]
            for t in range(4):
                tile(t % 2, 8, merged, ready=lambda h: pe.wait_ge(m_lo, L * 4 + (2 * h + 3)))
                if t:
                    sum_squares(t - 1)
            sum_squares(3)
            ffn()

        for t in range(3):
            m = P if t < 2 else NS
            for q in range(2):
                nm = f"out{t}_{q}"
                pe.wait_ge(nf_ready, 24 + 2 * q + 2)
                transposes(nm, (), [work[:, 4 * q + c, t * P:t * P + m] for c in range(4)],
                           [bk(nm)[0:m, c * P:(c + 1) * P] for c in range(4)])

    @block.scalar
    def _(act):
        cur = Count(1)
        r = [Count(1), Count(1)]
        nsum, nrm, soft_n, octet = Count(), Count(), Count(), Count(1)

        def wait(sem_value):
            act.wait_ge(*sem_value)

        def hi(s, h, nk, ahead):
            u, kh = 2 * s + h, nk // 2
            act.wait_ge(raw_loaded[u], cur.at(ahead) * 16)
            act.wait_ge(w_used[u], cur.at(ahead))
            act.activation(whi[u][:, 0:kh, :], wraw[u][:, 0:kh, :], ACT.Copy).then_inc(hi_done[u], 1)

        def products(s):
            act.wait_ge(w_used[2 * s + 1], cur.at(1))

        def pair(nxt, first=None, second=None):
            if first:
                first()
            if nxt:
                hi(0, 0, nxt[0], 1)
                hi(0, 1, nxt[0], 1)
                hi(1, 0, nxt[1], 1)
            if second:
                second()
            if nxt:
                hi(1, 1, nxt[1], 1)
            cur.next()

        def take(s, dst, func, n=T):
            def f():
                products(s)
                act.activation(dst, rs(s, n), func).then_inc(evac[s], 1)
                r[s].next()
            return f

        def square(g, s):
            act.wait_ge(evac[s], r[s].at())
            act.activation(work[:, 2 * g:2 * g + 2, :], x[:, 2 * g:2 * g + 2, :], ACT.Square).then_inc(sq_ready, 1)

        def deviation(n, width):
            act.wait_ge(sum_done, nsum.next())
            act.activation(std[:, 0:n], sums[:, 0:n], ACT.Sqrt, bias=epsc, scale=1.0 / width).then_inc(sum_read, 1)

        def norm():
            deviation(T, D)
            for g in range(4):
                act.wait_ge(nf_ready, nrm.next())
                act.activation(nh[:, 2 * g:2 * g + 2, :], work[:, 2 * g:2 * g + 2, :], ACT.Copy).then_inc(nh_ready, 1)

        def ffn(after):
            with repeat(act, UP, {cur: 1, r[0]: 1, r[1]: 1}) as i:
                def gated():
                    r[1].next()
                    act.wait_ge(evac[1], r[1].at())
                    act.activation(hh[:, ds(i * 2, 2), :], hf[:], ACT.Copy).then_inc(h_hi, 1)
                pair(FULL, take(0, sil[:], ACT.Silu), gated)
            for p in range(6):
                nxt = DOWN_PAIRS[p + 1] if p < 5 else after
                pair(nxt)
                if p % 3 == 1:
                    r[0].next()
                    square(2 * (p // 3), 0)
                if p % 3 == 2:
                    r[1].next()
                    square(2 * (p // 3) + 1, 1)

        for t in range(5):
            m = NS if t == 2 else P
            nm = f"in{t}_0"
            wait(fill(nm))
            dst = x[:, 0:4, t * P:t * P + m] if t < 3 else memn[:, 0:4, (t - 3) * P:(t - 2) * P]
            act.activation(dst, bk(nm)[:, :].rearrange("p (c m) -> p c m", c=4)[:, :, 0:m], ACT.Copy)\
                .then_inc(emptied_of(nm), 1)
        wait(fill("in4_1"))
        wait(empty("in4_1"))
        wait(empty("in4_0"))
        act.activation(work[:, :, 0:MEM], memn[:], ACT.Square).then_inc(sq_ready, 1)
        deviation(MEM, D)
        for g in range(4):
            act.activation(work[:, 2 * g:2 * g + 2, :], x[:, 2 * g:2 * g + 2, :], ACT.Square).then_inc(sq_ready, 1)
        act.wait_ge(memn_ready, 1)

        with repeat(act, DEPTH, {cur: PAIRS, r[0]: RES, r[1]: RES, nsum: SUMS, nrm: 12, soft_n: SOFT,
                                 octet: OCTETS}) as L:
            for s in range(2):
                for h in range(2):
                    hi(s, h, 8, 0)
            norm()
            ffn(FULL)

            act.wait_ge(memn_ready, 1)
            for k in range(8):
                a = act.activation(hh[:, k, 0:MEM], memn[:, k, :], ACT.Copy, scale=gains[:, ds(L * 8 + (G_MEM + k), 1)])
                if k % 2:
                    a.then_inc(mem_hi, 1)
            norm()
            pair(FULL, take(0, mkT[:, 0:2, :], ACT.Copy, MEM), take(1, mkT[:, 2:4, :], ACT.Copy, MEM))
            act.wait_ge(norm_ready, nrm.at())
            pair(FULL, take(0, work[:, 0:2, 0:MEM], ACT.Copy, MEM), take(1, work[:, 2:4, 0:MEM], ACT.Copy, MEM))

            pair(FULL, take(0, u_t[:, 0:2, :], ACT.Gelu), take(1, u_t[:, 2:4, :], ACT.Gelu))
            act.wait_ge(out_vn, L * 16 + 16)
            act.wait_ge(out_v, L * 32 + 16)
            for nm, dst in (("mk0", rows_a[:, 0, :]), ("mk1", rows_a[:, 1, :]), ("mv0", mvrow[:, 0, :]),
                            ("mv1", mvrow[:, 1, :])):
                wait(fill(nm, L))
                act.activation(dst, bk(nm)[:], ACT.Copy).then_inc(emptied_of(nm), 1)
            wait(empty("mk1", L))
            wait(empty("mv1", L))
            act.dma_start(A["new_mk"][L].rearrange("(t p) f -> p t f", p=P), rows_a[:, 0:2, :]).then_inc(out_mem, 16)
            act.dma_start(A["new_mv"][L].rearrange("(t p) f -> p t f", p=P), mvrow[:]).then_inc(out_mem, 16)
            pair(FULL, take(0, gv[:, 0:2, :], ACT.Gelu), take(1, gv[:, 2:4, :], ACT.Gelu))
            pair(FULL, take(0, work[:, 0:2, :], ACT.Copy), take(1, work[:, 2:4, :], ACT.Copy))
            nsum.next()
            act.wait_ge(sum_read, nsum.at())
            act.activation(lnsq[:], gv[:], ACT.Square).then_inc(xc_sq, 1)
            pair(FULL, take(0, work[:, 4:6, :], ACT.Copy), take(1, work[:, 6:8, :], ACT.Copy))
            deviation(T, SGU)
            wait(fill("rotq3", L))
            act.wait_ge(rot_ready, L * 8 + 4)
            pair(FULL, take(0, work[:, 0:2, :], ACT.Copy), take(1, work[:, 2:4, :], ACT.Copy))
            pair(MERGE, take(0, cq[:, 0:2, :], ACT.Copy), take(1, cq[:, 2:4, :], ACT.Copy))
            act.wait_ge(out_mem, L * 32 + 32)
            for nm, buf in (("vn", rows_a), ("k", krows), ("v", vrows)):
                for t in range(3):
                    m = P if t < 2 else NS
                    wait(fill(f"{nm}{t}", L))
                    act.activation(buf[0:m, t, :], bk(f"{nm}{t}")[0:m, :], ACT.Copy).then_inc(emptied_of(f"{nm}{t}"), 1)
                for t in range(3):
                    wait(empty(f"{nm}{t}", L))
                if nm == "vn":
                    act.dma_start(A["new_sv"][L], rows_a[0:NS, 2, :]).then_inc(out_vn, 16)
                else:
                    s_ = out_k if nm == "k" else out_v
                    act.dma_start(A[f"new_{nm}_p"][L].rearrange("(t p) f -> p t f", p=P), buf[:, 0:2, :]).then_inc(s_, 16)
                    act.dma_start(A[f"new_{nm}_s"][L], buf[0:NS, 2, :]).then_inc(s_, 16)

            def high(j, src):
                act.activation(hh[:, 4 * j:4 * j + 4, :], src, ACT.Copy).then_inc(y_hi, 1)

            act.wait_ge(ya_ready, L + 1)
            high(0, u_t[:])

            def gate():
                act.wait_ge(evac[1], r[1].at())
                take(0, gsil[:], ACT.Sigmoid)()

            for n in range(HEADS + 1):
                if n < HEADS:
                    act.wait_ge(p_max, soft_n.at(n + 1))
                    for qt in range(2):
                        a = act.activation(soft[n % 2][:, qt, :], soft[n % 2][:, qt, :], ACT.Exp,
                                           bias=stat[:, 4 * (n % 2) + qt:4 * (n % 2) + qt + 1],
                                           accum_out=stat[:, 4 * (n % 2) + 2 + qt:4 * (n % 2) + 3 + qt])
                    a.then_inc(p_exp, 1)
                if n:
                    if n % 3 == 1:
                        hi(0, 0, 8, 1)
                    elif n % 3 == 2:
                        gate()
                        hi(0, 1, 8, 1)
                    else:
                        hi(1, 0, 4, 1)
                        hi(1, 1, 4, 1)
                        cur.next()
                        r[1].next()
                    nm = f"PT{n - 1}"
                    k = 3 if n - 1 < 8 else 4
                    wait(fill(nm, L))
                    act.activation(ptp[(n - 1) % 2][:, 0:k, :],
                                   bk(nm)[:, 0:k * P].rearrange("p (k m) -> p k m", k=k), ACT.Copy)\
                        .then_inc(emptied_of(nm), 1)
            soft_n.n += HEADS

            with repeat(act, 2, {soft_n: 1, octet: 8}) as G:
                with repeat(act, 4, {octet: 1}) as jj:
                    for e in (0, 2, 4, 6):
                        wait(fill(f"kT{e}", L, G, jj))
                        act.wait_ge(page_used[(e - 2) % 8], octet.at(1 if e else 0))
                        act.activation(kTb[0][:], bk(f"kT{e}")[:, :].rearrange("p (c m) -> p c m", c=4), ACT.Copy)\
                            .then_inc(emptied_of(f"kT{e}"), 1)
                    octet.next()
                octet.n += 4
                act.wait_ge(p_max, soft_n.next())
                act.activation(S[:], S[:], ACT.Exp, bias=stat[:, 8:9], accum_out=stat[:, 9:10]).then_inc(p_exp, 1)
                for nm, dst, src in (("pT0", PT[:, 0:4, :], bk("pT0")[:, :].rearrange("p (j m) -> p j m", j=4)),
                                     ("pT1", PT[:, 4:8, :], bk("pT1")[:, :].rearrange("p (j m) -> p j m", j=4)),
                                     ("pTn", PT[0:NS, 8, :], bk("pTn")[0:NS, 0:P])):
                    wait(fill(nm, L, G))
                    act.activation(dst, src, ACT.Copy).then_inc(emptied_of(nm), 1)
            wait(empty("oT", L, 1))
            high(1, qk[:, 0:4, :])
            for g in range(2):
                for e in (0, 2, 4, 6):
                    nm = f"mkT{g}_{e}"
                    wait(fill(nm, L))
                    act.wait_ge(page_used[(e - 2) % 8], octet.at(1 if e else 0))
                    act.activation(kTb[0][:], bk(nm)[:, :].rearrange("p (c m) -> p c m", c=4), ACT.Copy)\
                        .then_inc(emptied_of(nm), 1)
                octet.next()
                act.wait_ge(p_max, soft_n.next())
                act.activation(S[:, g * MEM:(g + 1) * MEM], bk(f"ms{g}")[:, 0:MEM], ACT.Exp, bias=stat[:, 40 + g:41 + g],
                               scale=SC_MEM, accum_out=stat[:, 42 + g:43 + g]).then_inc(emptied_of(f"ms{g}"), 1)
            octet.n += 2
            for g in range(2):
                nm = f"mpT{g}"
                wait(fill(nm, L))
                act.activation(PT[:, 2 * g:2 * g + 2, :], bk(nm)[:, 0:MEM].rearrange("p (j m) -> p j m", j=2), ACT.Copy)\
                    .then_inc(emptied_of(nm), 1)
            wait(empty("moT1", L))
            high(2, cq[:])

            with repeat(act, 4, {cur: 1, r[0]: 1, r[1]: 1}):
                pair(MERGE, gate)
                r[1].next()

            def merge(g, nxt):
                pair(nxt, gate)
                r[1].next()
                act.wait_ge(m_f, L * 4 + g + 1)
                act.activation(hh[:, ds(g * 2 + 12, 2), :], acc[:, ds(g * 2, 2), :], ACT.Copy).then_inc(m_hi, 1)
            with repeat(act, 3, {cur: 1, r[0]: 1, r[1]: 1}) as g:
                merge(g, MERGE)
            merge(3, FULL)
            for p in range(2):
                pair(FULL)
                for s in range(2):
                    r[s].next()
                    square(2 * p + s, s)
            norm()
            ffn(None)
        deviation(T, D)
        for t in range(3):
            m = P if t < 2 else NS
            nm = f"out{t}_0"
            wait(fill(nm))
            act.activation(yout[t][0:m, 0:512], bk(nm)[0:m, :], ACT.Copy).then_inc(emptied_of(nm), 1)

    @block.vector
    def _(dve):
        cur = Count(1)
        r = [Count(1), Count(1)]
        nsum, nrm, hcnt, soft_n, step_n = Count(), Count(), Count(1), Count(), Count()
        octet = Count(1)

        def wait(sem_value):
            dve.wait_ge(*sem_value)

        def step(ins):
            ins.then_inc(dve_step, 1)
            dve.wait_ge(dve_step, step_n.next())

        def lo(s, h, nk, ahead):
            u, kh = 2 * s + h, nk // 2
            dve.wait_ge(hi_done[u], cur.at(ahead))
            dve.tensor_tensor(wlo[u][:, 0:kh, :], wraw[u][:, 0:kh, :], whi[u][:, 0:kh, :].bitcast(F32), ALU.subtract)\
                .then_inc(lo_done[u], 1)

        def products(s):
            dve.wait_ge(w_used[2 * s + 1], cur.at(1))

        def pair(nxt, first=None, second=None):
            if first:
                first()
            if nxt:
                lo(0, 0, nxt[0], 1)
                lo(0, 1, nxt[0], 1)
                lo(1, 0, nxt[1], 1)
            if second:
                second()
            if nxt:
                lo(1, 1, nxt[1], 1)
            cur.next()

        def add_to_x(g, s, slot, factor):
            def f():
                products(slot)
                xs_ = x[:, 2 * g:2 * g + 2, :]
                dve.scalar_tensor_tensor(xs_, rs(s), factor, xs_, ALU.mult, ALU.add).then_inc(evac[s], 1)
                r[s].next()
            return f

        def norm(gain, split=True):
            dve.wait_ge(sum_read, nsum.next())
            step(dve.reciprocal(rstd[:], std[:]))

            def low(g):
                dve.wait_ge(nh_ready, nrm.at(g + 1))
                dve.tensor_tensor(nl[:, 2 * g:2 * g + 2, :], work[:, 2 * g:2 * g + 2, :],
                                  nh[:, 2 * g:2 * g + 2, :].bitcast(F32), ALU.subtract).then_inc(norm_ready, 1)
            for g in range(4):
                for k in (2 * g, 2 * g + 1):
                    i = dve.scalar_tensor_tensor(work[:, k, :], x[:, k, :], gains[:, gain(k)], rstd[:], ALU.mult, ALU.mult)
                i.then_inc(nf_ready, 1)
                if split and g:
                    low(g - 1)
            if split:
                low(3)
                nrm.n += 4

        def ffn(after):
            with repeat(dve, UP, {cur: 1, r[0]: 1, r[1]: 1, hcnt: 1, step_n: 0}) as i:
                def gate():
                    products(1)
                    dve.wait_ge(evac[0], r[0].next())
                    dve.wait_ge(h_ready, hcnt.at())
                    dve.tensor_tensor(hf[:], sil[:], rs(1), ALU.mult).then_inc(evac[1], 1)
                    r[1].next()
                pair(FULL, None, gate)
                dve.wait_ge(h_hi, hcnt.at())
                hcnt.next()
                dve.tensor_tensor(hl[:, ds(i * 2, 2), :], hf[:], hh[:, ds(i * 2, 2), :].bitcast(F32), ALU.subtract)\
                    .then_inc(h_ready, 1)
            for p in range(6):
                nxt = DOWN_PAIRS[p + 1] if p < 5 else after
                g = 2 * (p // 3)
                pair(nxt, add_to_x(g, 0, 0, 0.5) if p % 3 == 1 else None, add_to_x(g + 1, 1, 1, 0.5) if p % 3 == 2 else None)

        wait(fill("gainT"))
        dve.tensor_copy(gains[:], bk("gainT")[:, 0:G_ALL]).then_inc(emptied_of("gainT"), 1)
        for t in range(5):
            m = NS if t == 2 else P
            nm = f"in{t}_1"
            wait(fill(nm))
            dst = x[:, 4:8, t * P:t * P + m] if t < 3 else memn[:, 4:8, (t - 3) * P:(t - 2) * P]
            dve.tensor_copy(dst, bk(nm)[:, :].rearrange("p (c m) -> p c m", c=4)[:, :, 0:m]).then_inc(emptied_of(nm), 1)
        dve.wait_ge(sum_read, nsum.next())
        step(dve.reciprocal(rstd[:, 0:MEM], std[:, 0:MEM]))
        dve.tensor_tensor(memn[:], memn[:], rstd[:, 0:MEM].unsqueeze(1).broadcast_to([P, KD, MEM]), ALU.mult)\
            .then_inc(memn_ready, 1)
        dve.wait_ge(*empty("gainT"))

        with repeat(dve, DEPTH, {cur: PAIRS, r[0]: RES, r[1]: RES, nsum: SUMS, nrm: 12, hcnt: 2 * UP, soft_n: SOFT,
                                 step_n: STEPS, octet: OCTETS}) as L:
            def layer_gain(base):
                return lambda k: ds(L * 8 + (base + k), 1)
            for s in range(2):
                for h in range(2):
                    lo(s, h, 8, 0)
            norm(layer_gain(G_FFN1))
            ffn(FULL)

            dve.wait_ge(memn_ready, 1)
            for k in range(8):
                if k % 2 == 0:
                    dve.wait_ge(mem_hi, L * 4 + (k // 2 + 1))
                i = dve.scalar_tensor_tensor(hl[:, k, 0:MEM], memn[:, k, :], gains[:, ds(L * 8 + (G_MEM + k), 1)],
                                             hh[:, k, 0:MEM].bitcast(F32), ALU.mult, ALU.subtract)
                if k % 2:
                    i.then_inc(mem_ready, 1)
            norm(layer_gain(G_MIX))
            pair(FULL)
            pair(FULL)
            pair(FULL)
            r[0].n += 3
            r[1].n += 3
            wait(fill("wmT", L))
            tril = cst[:, C_TRIL:C_TRIL + P].unsqueeze(1).broadcast_to([P, 4, P])
            dve.tensor_tensor(wmT[:], bk("wmT")[:, :].rearrange("p (g i) -> p g i", g=4), tril, ALU.mult)\
                .then_inc(emptied_of("wmT"), 1)
            pair(FULL)
            pair(FULL)
            r[0].n += 2
            r[1].n += 2
            wait(fill("rep", L))
            for g in range(4):
                src = bk("rep")[0:NS, 4 * g:4 * g + 4].unsqueeze(1).broadcast_to([NS, DEC_B, DEC_T])
                msk = cst[0:NS, C_BD:C_BD + NS].rearrange("p (b i) -> p b i", b=DEC_B)
                i = dve.tensor_tensor(bd[:, g, :].rearrange("p (b i) -> p b i", b=DEC_B), src, msk, ALU.mult)
            i.then_inc(emptied_of("rep"), 1)
            dve.wait_ge(sum_done, nsum.at(1))
            dve.scalar_tensor_tensor(gv[:], sums[:, 0:T].unsqueeze(1).broadcast_to([P, 4, T]), -1.0 / SGU, gv[:],
                                     ALU.mult, ALU.add).then_inc(sum_read, 1)
            nsum.next()
            cosb = cst[:, C_COS:C_COS + T].unsqueeze(1).broadcast_to([P, 4, T])
            dve.wait_ge(evac[0], r[0].at())
            dve.wait_ge(evac[1], r[1].at())
            step(dve.tensor_tensor(qk[:, 0:4, :], work[:, 0:4, :], cosb, ALU.mult))
            pair(FULL)
            r[0].next()
            r[1].next()

            def rotate(which, c):
                nm, o = f"rot{which}{c}", 0 if which == "q" else 4
                wait(fill(nm, L))
                tmp = rtmp[c % 2]
                if o + c >= 2:
                    dve.wait_ge(rot_ready, L * 8 + (o + c - 1))
                dve.tensor_tensor(tmp[:], bk(nm)[:, 0:T], cst[:, C_SIN:C_SIN + T], ALU.mult).then_inc(emptied_of(nm), 1)
                wait(empty(nm, L))
                dve.tensor_tensor(qk[:, o + c, :], qk[:, o + c, :], tmp[:], ALU.add).then_inc(rot_ready, 1)
            dve.wait_ge(evac[0], r[0].at())
            dve.wait_ge(evac[1], r[1].at())
            step(dve.tensor_tensor(qk[:, 4:8, :], work[:, 4:8, :], cosb, ALU.mult))
            for c in range(4):
                rotate("q", c)
            dve.wait_ge(sum_read, nsum.next())
            step(dve.reciprocal(rstd[:], std[:]))
            step(dve.tensor_tensor(gv[:], gv[:], rstd[:].unsqueeze(1).broadcast_to([P, 4, T]), ALU.mult))
            for k in range(4):
                i = dve.tensor_scalar(gv[:, k, :], gv[:, k, :], gains[:, ds(L * 4 + (G_LNG + k), 1)],
                                      gains[:, ds(L * 4 + (G_LNB + k), 1)], ALU.mult, ALU.add)
            i.then_inc(vn_ready, 1)
            pair(FULL)
            for c in range(4):
                rotate("k", c)
            pair(MERGE)
            r[0].n += 2
            r[1].n += 2
            dve.wait_ge(ld_sb, L * 16 + 16)
            tmp = rtmp[0]
            for g in range(4):
                nm = f"sgu{g}"
                wait(fill(nm, L))
                dve.tensor_tensor(tmp[:, 0:SEQ].rearrange("p (t i) -> p t i", t=2),
                                  bk(nm)[:, 0:SEQ].rearrange("p (t i) -> p t i", t=2),
                                  sgb[:, g, :].unsqueeze(1).broadcast_to([P, 2, P]), ALU.add)
                dve.tensor_tensor(tmp[:, SEQ:T].rearrange("p (b i) -> p b i", b=DEC_B),
                                  bk(nm)[:, SEQ:T].rearrange("p (b i) -> p b i", b=DEC_B),
                                  sgb[:, g, 0:DEC_T].unsqueeze(1).broadcast_to([P, DEC_B, DEC_T]), ALU.add)\
                    .then_inc(emptied_of(nm), 1)
                wait(empty(nm, L))
                i = dve.tensor_tensor(u_t[:, g, :], u_t[:, g, :], tmp[:], ALU.mult)
                if g < 3:
                    step(i)
            i.then_inc(ya_ready, 1)

            def low(j, src):
                dve.wait_ge(y_hi, L * 3 + (j + 1))
                dve.tensor_tensor(hl[:, 4 * j:4 * j + 4, :], src, hh[:, 4 * j:4 * j + 4, :].bitcast(F32), ALU.subtract)\
                    .then_inc(y_lo, 1)
            low(0, u_t[:])

            mask = cst[:, C_CAUSAL:C_CAUSAL + 512].rearrange("p (q k) -> p q k", q=2)
            for n in range(HEADS + 2):
                if n < HEADS:
                    nm, sm, o = f"S{n}", soft[n % 2], 4 * (n % 2)
                    wait(fill(nm, L))
                    if n >= 2:
                        wait(fill(f"PT{n - 2}", L))
                    src = bk(nm)[:, :].rearrange("p (q k) -> p q k", q=2)
                    if n < 8:
                        dve.scalar_tensor_tensor(sm[:], src, SC_MOBA, mask, ALU.mult, ALU.add).then_inc(emptied_of(nm), 1)
                    else:
                        dve.tensor_scalar(sm[:], src, SC_MEM, None, ALU.mult).then_inc(emptied_of(nm), 1)
                    wait(empty(nm, L))
                    dve.tensor_reduce(stat[:, o:o + 2], sm[:], AX.X, ALU.max, negate=True).then_inc(p_max, 1)
                if 1 <= n <= HEADS:
                    m, sm, o = n - 1, soft[(n - 1) % 2], 4 * ((n - 1) % 2)
                    dve.wait_ge(p_exp, L * (HEADS + 2) + (m + 1))
                    step(dve.reciprocal(stat[:, o + 2:o + 4], stat[:, o + 2:o + 4]))
                    for qt in range(2):
                        i = dve.tensor_scalar(sm[:, qt, :], sm[:, qt, :], stat[:, o + 2 + qt:o + 3 + qt], None, ALU.mult)
                    i.then_inc(p_nrm, 1)
                    if n % 3 == 1:
                        lo(0, 0, 8, 1)
                    elif n % 3 == 2:
                        lo(0, 1, 8, 1)
                    else:
                        g = n // 3 - 1
                        products(1)
                        dve.wait_ge(evac[0], r[0].next())
                        dve.tensor_tensor(acc[:, 2 * g:2 * g + 2, :], gsil[:], rs(1), ALU.mult).then_inc(evac[1], 1)
                        r[1].next()
                        lo(1, 0, 4, 1)
                        lo(1, 1, 4, 1)
                        cur.next()
                if n >= 2 and (n - 2 >= 8 or n % 2 == 1):
                    m = n - 2
                    nm = f"O{m - m % 2}" if m < 8 else f"O{m}"
                    wait(fill(nm, L))
                    dst = qk[:, m // 2, 0:SEQ] if m < 8 else cq[:, m - 8, 0:SEQ]
                    dve.tensor_copy(dst, bk(nm)[:, 0:SEQ]).then_inc(emptied_of(nm), 1)
            soft_n.n += HEADS

            def col(a, n=1):
                return stat[:, a:a + n]

            dve.memset(qbd[0][:], 0.0).then_inc(dve_step, 1)
            step_n.next()
            with repeat(dve, 2, {soft_n: 1, step_n: 11, octet: 8}) as G:
                dve.wait_ge(dve_step, step_n.at())
                for c in range(4):
                    for hh_ in range(2):
                        lo_, hi_ = HD * hh_, HD * hh_ + HD
                        i = dve.tensor_scalar(qbd[0][lo_:hi_, c, :, 8 * c + 4 * hh_:8 * c + 4 * hh_ + 4],
                                              qk[lo_:hi_, c, ds(G * 16 + SEQ, 16)].rearrange("p (b t) -> p b t", b=4),
                                              1.0, None, ALU.mult)
                i.then_inc(qbd_ready, 1)
                with repeat(dve, 4, {octet: 1, step_n: 1}) as jj:
                    for e in (1, 3, 5, 7):
                        nm = f"kT{e}"
                        wait(fill(nm, L, G, jj))
                        dve.wait_ge(page_used[(e - 2) % 8], octet.at(1 if e > 1 else 0))
                        dve.tensor_copy(kTb[1][:], bk(nm)[:, :].rearrange("p (c m) -> p c m", c=4)).then_inc(emptied_of(nm), 1)
                    dve.wait_ge(page_used[7], octet.at(1))
                    blk = S[:, ds(jj * 256, 256)]
                    dve.tensor_scalar(blk, bk("sS")[:, 0:256], SC_MOBA, None, ALU.mult).then_inc(emptied_of("sS"), 1)
                    wait(empty("sS", L, G, jj))
                    step(dve.tensor_reduce(stat[:, ds(jj + 16, 1)], blk, AX.X, ALU.add))
                    octet.next()
                octet.n += 4
                wait(fill("newS", L, G))
                dve.scalar_tensor_tensor(S[:, PAST:PAST + NS], bk("newS")[:, 0:NS], SC_MOBA,
                                         cst[:, ds(G * NS + C_NEWMASK, NS)], ALU.mult, ALU.add).then_inc(emptied_of("newS"), 1)
                step(dve.tensor_reduce(col(20), col(16, 4), AX.X, ALU.min))
                step(dve.tensor_scalar(col(24, 4), col(16, 4), col(20), None, ALU.is_equal))
                step(dve.tensor_tensor(col(28, 4), col(24, 4), cst[:, C_BLOCKW:C_BLOCKW + 4], ALU.mult))
                step(dve.tensor_reduce(col(21), col(28, 4), AX.X, ALU.max))
                step(dve.tensor_scalar(col(32, 4), col(28, 4), col(21), NEG, ALU.is_equal, ALU.mult))
                for n in range(4):
                    i = dve.tensor_scalar(S[:, n * 256:(n + 1) * 256], S[:, n * 256:(n + 1) * 256], col(32 + n), None,
                                          ALU.add)
                step(i)
                dve.tensor_reduce(col(8), S[:], AX.X, ALU.max, negate=True).then_inc(p_max, 1)
                dve.wait_ge(p_exp, L * (HEADS + 2) + (G + (HEADS + 1)))
                step(dve.reciprocal(col(10), col(9)))
                dve.tensor_scalar(S[:], S[:], col(10), None, ALU.mult).then_inc(p_nrm, 1)
                dve.wait_ge(page_used[7], octet.at())
                dve.tensor_copy(S[:, 0:512], bk("oG")[:, :]).then_inc(emptied_of("oG"), 1)
                wait(fill("oT", L, G))
                o4 = bk("oT")[:, 0:P].rearrange("p (c b r) -> p c b r", b=4, c=4)
                for hh_ in range(2):
                    lo_, hi_ = HD * hh_, HD * hh_ + HD
                    dst = qk[lo_:hi_, 0:4, ds(G * 16 + SEQ, 16)].rearrange("p c (b t) -> p c b t", b=4)
                    i = dve.tensor_scalar(dst, o4[lo_:hi_, :, :, 4 * hh_:4 * hh_ + 4], 1.0, None, ALU.mult)
                i.then_inc(emptied_of("oT"), 1)
                soft_n.next()
            low(1, qk[:, 0:4, :])

            dve.memset(qbd[0][:], 0.0)
            step(dve.memset(qbd[1][:], 0.0))
            for g in range(2):
                for c in range(4):
                    i = dve.tensor_copy(qbd[g][:, c, :, 8 * c:8 * c + 4],
                                        cq[:, c, SEQ + 16 * g:SEQ + 16 * g + 16].rearrange("p (b t) -> p b t", b=4))
                i.then_inc(qbd_ready, 1)
            for g in range(2):
                for e in (1, 3, 5, 7):
                    nm = f"mkT{g}_{e}"
                    wait(fill(nm, L))
                    dve.wait_ge(page_used[(e - 2) % 8], octet.at(1 if e > 1 else 0))
                    dve.tensor_copy(kTb[1][:], bk(nm)[:, :].rearrange("p (c m) -> p c m", c=4)).then_inc(emptied_of(nm), 1)
                octet.next()
                dve.wait_ge(page_used[7], octet.at())
                step(dve.tensor_reduce(col(38 + g), bk(f"ms{g}")[:, 0:MEM], AX.X, ALU.max, negate=True))
                dve.tensor_scalar(col(40 + g), col(38 + g), SC_MEM, None, ALU.mult).then_inc(p_max, 1)
            for g in range(2):
                wait(empty(f"ms{g}", L))
                step(dve.reciprocal(col(44 + g), col(42 + g)))
                s_ = S[:, g * MEM:(g + 1) * MEM]
                dve.tensor_scalar(s_, s_, col(44 + g), None, ALU.mult).then_inc(p_nrm, 1)
                soft_n.next()
            for g in range(2):
                octet.next()
                dve.wait_ge(page_used[7], octet.at())
                dve.tensor_copy(S[:, 512 * g:512 * g + 512], bk(f"mo{g}")[:, :]).then_inc(emptied_of(f"mo{g}"), 1)
            for g in range(2):
                wait(fill(f"moT{g}", L))
                dve.tensor_copy(cq[:, :, SEQ + 16 * g:SEQ + 16 * g + 16].rearrange("p c (b t) -> p c b t", b=4),
                                bk(f"moT{g}")[:, 0:P].rearrange("p (c b r) -> p c b r", b=4, c=4)[:, :, :, 0:4])\
                    .then_inc(emptied_of(f"moT{g}"), 1)
            low(2, cq[:])

            def gated(g, j):
                def f():
                    products(1)
                    dve.wait_ge(evac[0], r[0].next())
                    dve.tensor_tensor(gtmp[:], gsil[:], rs(1), ALU.mult).then_inc(evac[1], 1)
                    dve.wait_ge(evac[1], r[1].next())
                    to = acc[:, ds(g * 2, 2), :]
                    i = dve.tensor_tensor(to, to, gtmp[:], ALU.add)
                    if j == 1:
                        step(i)
                    else:
                        i.then_inc(m_f, 1)
                return f
            with repeat(dve, 4, {cur: 1, r[0]: 1, r[1]: 1, step_n: 1}) as g:
                pair(MERGE, None, gated(g, 1))

            def merge(g, nxt):
                pair(nxt, None, gated(g, 2))
                dve.wait_ge(m_hi, L * 4 + g + 1)
                dve.tensor_tensor(hl[:, ds(g * 2 + 12, 2), :], acc[:, ds(g * 2, 2), :],
                                  hh[:, ds(g * 2 + 12, 2), :].bitcast(F32), ALU.subtract).then_inc(m_lo, 1)
            with repeat(dve, 3, {cur: 1, r[0]: 1, r[1]: 1}) as g:
                merge(g, MERGE)
            merge(3, FULL)
            for p in range(2):
                pair(FULL, add_to_x(2 * p, 0, 0, 1.0), add_to_x(2 * p + 1, 1, 1, 1.0))
            norm(layer_gain(G_FFN2))
            ffn(None)
        norm(lambda k: slice(G_FINAL + k, G_FINAL + k + 1), split=False)
        for t in range(3):
            m = P if t < 2 else NS
            nm = f"out{t}_1"
            wait(fill(nm))
            dve.tensor_copy(yout[t][0:m, 512:1024], bk(nm)[0:m, :]).then_inc(emptied_of(nm), 1)

    @block.sync
    def _(sp):
        nc.disable_value_cache = True
        pair = Count(1)

        def load(s, src, nk):
            for h in range(2):
                u, kh = 2 * s + h, nk // 2
                sp.wait_ge(lo_done[u], pair.at())
                sp.dma_start(wraw[u][:, 0:kh, :], src[:, h * kh:(h + 1) * kh, :]).then_inc(raw_loaded[u], 16)
            if s == 1:
                pair.next()

        def ffn(L, w1, w3, w2):
            with repeat(sp, UP, {pair: 1}) as i:
                load(0, wt[w1][L][:, :, ds(i * W, W)], 8)
                load(1, wt[w3][L][:, :, ds(i * W, W)], 8)
            for t in range(12):
                g, part = t // 3, t % 3
                nk = DOWN_NK[part]
                load(t % 2, wt[w2][L][:, 8 * part:8 * part + nk, g * W:(g + 1) * W], nk)

        sp.dma_start(cst[:], A["const"]).then_inc(ld_const, 16)
        sp.dma_start(xrow[0][:], A["x_prompt"][0, 0:P, :]).then_inc(ld_x[0], 16)
        sp.dma_start(xrow[1][:], A["x_prompt"][0, P:2 * P, :]).then_inc(ld_x[1], 16)
        sp.dma_start(xrow[2][0:NS, :], A["x_sample"].rearrange("b t d -> (b t) d")).then_inc(ld_x[2], 16)
        sp.dma_start(xrow[3][:], A["mem_prompt"][0, 0:P, :]).then_inc(ld_x[3], 16)
        sp.dma_start(xrow[4][:], A["mem_prompt"][0, P:2 * P, :]).then_inc(ld_x[4], 16)
        sp.wait_ge(ld_page, 16)
        octet = Count(1)

        def load_page(e, src):
            sp.wait_ge(page_used[e], octet.at())
            sp.dma_start(page[e][:], src).then_inc(page_loaded[e], 16)

        with repeat(sp, DEPTH, {pair: PAIRS, octet: OCTETS}) as L:
            ffn(L, "ffn1_w1", "ffn1_w3", "ffn1_w2")
            sp.wait_ge(h_ready, L * (2 * UP) + (UP + 1))
            sp.dma_start(swrow[:], A["sgu_w"][L].rearrange("g i j -> i g j")).then_inc(ld_sw, 16)
            sp.dma_start(sgb[:], A["sgu_b"][L].unsqueeze(0).broadcast_to([P, 4, P])).then_inc(ld_sb, 16)
            for t in range(4):
                load(t % 2, wt["w_mem_kv"][L][:, :, t * W:(t + 1) * W], 8)
            for t in range(12):
                load(t % 2, wt["w_in"][L][:, :, t * W:(t + 1) * W], 8)
            def gate_pair(g, j):
                load(0, wt["w_in"][L][:, :, ds(g * W + (GATE0 + j * D), W)], 8)
                load(1, wt[branch_w[j]][L][:, :, ds(g * W, W)], 4)
            for g in range(4):
                gate_pair(g, 0)
            gate_pair(0, 1)
            with repeat(sp, 2, {octet: 8}) as G:
                for cache in (A["cache_k"], A["cache_v"]):
                    with repeat(sp, 4, {octet: 1}) as jj:
                        for e in range(8):
                            if e == 0:
                                _, pages = nc.values_load_multi_w_load_instructions(
                                    ptab[0:1, :].rearrange("o (b j) -> o b j", j=8)[:, ds(G * 4, 4), ds(jj * 2, 2)],
                                    engines=(mybir.EngineType.SP,), min_val=0,
                                    max_val=A["cache_k"].shape[1] - 1)
                            pg = pages[2 * (e % 4) + e // 4]
                            if e == 0:
                                sp.wait_ge(out_k, L * 32 + 32)
                                for t in range(3):
                                    sp.wait_ge(*empty(f"v{t}", L))
                            load_page(e, cache[L, pg].rearrange("s h d -> s (h d)"))
                        octet.next()
            for cache in (A["cache_mem_k"], A["cache_mem_v"]):
                for g in range(2):
                    for e in range(8):
                        src = cache[L][4 * g + e // 2].rearrange("m h d -> m (h d)")
                        load_page(e, src[(e % 2) * P:(e % 2) * P + P, :])
                    octet.next()
            with repeat(sp, 3, {pair: 1}) as g:
                gate_pair(g + 1, 1)
            with repeat(sp, 4, {pair: 1}) as g:
                gate_pair(g, 2)
            for t in range(4):
                load(t % 2, wt["w_o"][L][:, :, t * W:(t + 1) * W], 8)
            ffn(L, "ffn2_w1", "ffn2_w3", "ffn2_w2")
        sp.wait_ge(out_mem, DEPTH * 32)
        sp.wait_ge(out_k, DEPTH * 32)
        sp.wait_ge(out_v, DEPTH * 32 + 16)
        sp.wait_ge(out_vn, DEPTH * 16 + 16)
        for t in range(3):
            for q in range(2):
                sp.wait_ge(*empty(f"out{t}_{q}"))
            dst = A["y_prompt"][t * P:(t + 1) * P, :] if t < 2 else A["y_sample"]
            sp.dma_start(dst, yout[t][0:P if t < 2 else NS, :]).then_inc(out_y, 16)
        sp.wait_ge(out_y, 48)

    nc.disable_value_cache = False

    @block.gpsimd
    def _(pool):
        for s_ in (*lo_done, *w_used, *evac, *emptied, *page_used, h_ready, m_lo):
            pool.sem_inc(s_, 1)
        for s_ in (out_v, out_vn):
            pool.sem_inc(s_, 16)
        pool.dma_start(ptab[:], A["page_table"].rearrange("(o b) j -> o (b j)", o=1)).then_inc(ld_page, 16)
        for name, o, n in (("ffn1_norm", G_FFN1, 16), ("mix_norm", G_MIX, 16), ("ffn2_norm", G_FFN2, 16),
                           ("mem_norm", G_MEM, 16), ("sgu_ln_g", G_LNG, 8), ("sgu_ln_b", G_LNB, 8)):
            pool.dma_start(grow[o:o + n, :], A[name].rearrange("l (k p) -> (l k) p", p=P)).then_inc(ld_gain, 16)
        pool.dma_start(grow[G_FINAL:G_FINAL + 8, :], A["final_norm"].rearrange("(k p) -> k p", p=P)).then_inc(ld_gain, 16)

    st.close()


_INS = ["x_prompt", "x_sample", "mem_prompt", "cache_k", "cache_v", "cache_mem_k", "cache_mem_v", "page_table",
        "ffn1_norm", "ffn1_w1", "ffn1_w3", "ffn1_w2", "mix_norm", "w_in", "sgu_ln_g", "sgu_ln_b", "sgu_w", "sgu_b",
        "mem_norm", "w_mem_kv", "w_a_out", "w_b_out", "w_c_out", "w_o", "ffn2_norm", "ffn2_w1", "ffn2_w3", "ffn2_w2",
        "final_norm"]
_OUTS = [("y_prompt", (SEQ, D), (1, SEQ, D)), ("y_sample", (NS, D), (DEC_B, DEC_T, D)),
         ("new_k_p", (DEPTH, SEQ, 512), (DEPTH, 1, SEQ, 8, 64)), ("new_v_p", (DEPTH, SEQ, 512), (DEPTH, 1, SEQ, 8, 64)),
         ("new_mk", (DEPTH, MEM, 512), (DEPTH, 1, MEM, 4, 128)), ("new_mv", (DEPTH, MEM, 512), (DEPTH, 1, MEM, 4, 128)),
         ("new_k_s", (DEPTH, NS, 512), (DEPTH, DEC_B, DEC_T, 8, 64)),
         ("new_v_s", (DEPTH, NS, 512), (DEPTH, DEC_B, DEC_T, 8, 64)),
         ("new_sv", (DEPTH, NS, 512), (DEPTH, DEC_B, DEC_T, 512))]


def kernel(**inputs):
    import concourse.bacc as _bacc
    from concourse.bass_utils import run_bass_kernel_spmd as _run

    nc = _bacc.Bacc("TRN2", target_bir_lowering=False, num_devices=1)
    arrays, args = {}, {}
    for name in _INS:
        a = np.ascontiguousarray(inputs[name])
        arrays[f"in_{name}"] = a
        args[name] = nc.dram_tensor(f"in_{name}", a.shape, mybir.dt.from_np(a.dtype), kind="ExternalInput").ap()
    arrays["in_const"] = constants()
    args["const"] = nc.dram_tensor("in_const", arrays["in_const"].shape, F32, kind="ExternalInput").ap()
    for name, shape, _ in _OUTS:
        args[name] = nc.dram_tensor(f"out_{name}", shape, F32, kind="ExternalOutput").ap()
    build(nc, args)
    r = _run(nc, [arrays], core_ids=[0])
    return tuple(np.asarray(r.results[0][f"out_{name}"]).reshape(shape) for name, _, shape in _OUTS)
```
